# Optimizing a Trainium2 kernel written in Bass

```python
import math
import jax, jax.numpy as jnp
from jax import lax
import numpy as np

D_MODEL = 1024
BATCH = 1
SEQ = 512
DEPTH = 1

N_MEM = 256
GM_GROUPS = 4
GM_DIM = 128
GM_CHUNK = 128
GM_WIDTH = GM_GROUPS * GM_DIM
DN_HEADS = 4
DN_DK = 128
DN_DV = 128
DN_CHUNK = 64
CONV_W = 4
DN_QK = DN_HEADS * DN_DK
DN_V = DN_HEADS * DN_DV
MIX_WIDTH = GM_WIDTH + DN_V
D_FF = 4 * D_MODEL
XA_HEADS = 4
XA_DIM = D_MODEL // XA_HEADS
EPS = 1e-6
IN_SIZES = (GM_WIDTH, GM_WIDTH, DN_QK, DN_QK, DN_V, DN_V, DN_HEADS, DN_HEADS)
D_IN = 2 * GM_WIDTH + 2 * DN_QK + 2 * DN_V + 2 * DN_HEADS


def rmsnorm(x, g):
    xf = x.astype(jnp.float32)
    y = xf * lax.rsqrt(jnp.mean(xf * xf, axis=-1, keepdims=True) + EPS)
    return (y * g.astype(jnp.float32)).astype(x.dtype)

def layernorm(x, g, b):
    xf = x.astype(jnp.float32)
    mu = jnp.mean(xf, axis=-1, keepdims=True)
    var = jnp.mean(jnp.square(xf - mu), axis=-1, keepdims=True)
    y = (xf - mu) * lax.rsqrt(var + EPS)
    return (y * g.astype(jnp.float32) + b.astype(jnp.float32)).astype(x.dtype)

def l2norm(x):
    return x * lax.rsqrt(jnp.sum(x * x, axis=-1, keepdims=True) + EPS)

def split_cols(t, sizes):
    idx = [int(i) for i in np.cumsum(np.array(sizes))[:-1]]
    return jnp.split(t, idx, axis=-1)

def chunk_spatial_gating(u, v, ln_g, ln_b, w_s, b_s):
    bsz, s, _ = u.shape
    nc = s // GM_CHUNK
    u = jax.nn.gelu(u).reshape(bsz, nc, GM_CHUNK, GM_GROUPS, GM_DIM)
    v = jax.nn.gelu(v).reshape(bsz, nc, GM_CHUNK, GM_GROUPS, GM_DIM)
    v = layernorm(v, ln_g, ln_b)
    causal = jnp.tril(jnp.ones((GM_CHUNK, GM_CHUNK), dtype=bool))
    w = jnp.where(causal, w_s, jnp.zeros_like(w_s))
    mixed = jnp.einsum('gts,bcsgd->bctgd', w, v) + jnp.transpose(b_s)[None, None, :, :, None]
    return (u * mixed).reshape(bsz, s, GM_WIDTH)

def causal_dwconv(x, w):
    c = x.shape[-1]
    return lax.conv_general_dilated(
        x, w[:, None, :].astype(x.dtype), window_strides=(1,), padding=[(CONV_W - 1, 0)],
        dimension_numbers=('NWC', 'WIO', 'NWC'), feature_group_count=c)

def gated_delta_rule(q, k, v, g, beta):
    f32 = jnp.float32
    bsz, s, h, dk = q.shape
    dv = v.shape[-1]
    c = DN_CHUNK
    n = s // c

    def chunks(t):
        return t.astype(f32).reshape(bsz, n, c, h, -1).transpose(0, 3, 1, 2, 4)

    q = chunks(q) * (dk ** -0.5)
    k = chunks(k)
    v = chunks(v)
    beta = beta.astype(f32).reshape(bsz, n, c, h).transpose(0, 3, 1, 2)[..., None]
    g = g.astype(f32).reshape(bsz, n, c, h).transpose(0, 3, 1, 2)
    decay = jnp.cumsum(g, axis=-1)
    tri = jnp.tril(jnp.ones((c, c), dtype=bool))
    strict = jnp.tril(jnp.ones((c, c), dtype=bool), -1)
    lmask = jnp.exp(jnp.where(tri, decay[..., :, None] - decay[..., None, :], -jnp.inf))

    k_beta = k * beta
    v_beta = v * beta
    m = jnp.where(strict, jnp.einsum('bhnid,bhnjd->bhnij', k_beta, k) * lmask, 0.0)
    a = m + jnp.eye(c, dtype=f32)
    rhs = jnp.concatenate([v_beta, k_beta * jnp.exp(decay)[..., None]], axis=-1)
    sol = lax.linalg.triangular_solve(a, rhs, left_side=True, lower=True, unit_diagonal=True)
    u_c = sol[..., :dv]
    w_c = sol[..., dv:]

    qk = jnp.where(tri, jnp.einsum('bhnid,bhnjd->bhnij', q, k) * lmask, 0.0)
    q_dec = q * jnp.exp(decay)[..., None]
    k_dec = k * jnp.exp(decay[..., -1:] - decay)[..., None]
    chunk_decay = jnp.exp(decay[..., -1])

    xs = tuple(jnp.moveaxis(t, 2, 0) for t in (qk, q_dec, k_dec, u_c, w_c, chunk_decay))

    def step(state, inp):
        qk_i, q_dec_i, k_dec_i, u_i, w_i, cd_i = inp
        v_new = u_i - jnp.einsum('bhck,bhkv->bhcv', w_i, state)
        o = jnp.einsum('bhck,bhkv->bhcv', q_dec_i, state) + jnp.einsum('bhij,bhjv->bhiv', qk_i, v_new)
        state = state * cd_i[..., None, None] + jnp.einsum('bhck,bhcv->bhkv', k_dec_i, v_new)
        return state, o

    s0 = jnp.zeros((bsz, h, dk, dv), f32)
    _, o = lax.scan(step, s0, xs)
    return o.transpose(1, 0, 3, 2, 4).reshape(bsz, s, h, dv)

def hybrid_mixer(h, w_in, gm_ln_g, gm_ln_b, gm_ws, gm_bs, dn_conv, dn_a_log, dn_dt_bias, dn_onorm, w_out):
    bsz, s, _ = h.shape
    proj = h @ w_in
    gu, gv, q, k, v, gate, b_logit, a_logit = split_cols(proj, IN_SIZES)

    y_a = chunk_spatial_gating(gu, gv, gm_ln_g, gm_ln_b, gm_ws, gm_bs)

    qkv = jax.nn.silu(causal_dwconv(jnp.concatenate([q, k, v], axis=-1), dn_conv))
    q, k, v = split_cols(qkv, (DN_QK, DN_QK, DN_V))
    q = l2norm(q.astype(jnp.float32).reshape(bsz, s, DN_HEADS, DN_DK))
    k = l2norm(k.astype(jnp.float32).reshape(bsz, s, DN_HEADS, DN_DK))
    v = v.reshape(bsz, s, DN_HEADS, DN_DV)
    beta = jax.nn.sigmoid(b_logit.astype(jnp.float32))
    g = -jnp.exp(dn_a_log.astype(jnp.float32)) * jax.nn.softplus(
        a_logit.astype(jnp.float32) + dn_dt_bias.astype(jnp.float32))
    o = gated_delta_rule(q, k, v, g, beta)
    o = rmsnorm(o, dn_onorm) * jax.nn.silu(gate.astype(jnp.float32).reshape(bsz, s, DN_HEADS, DN_DV))
    y_b = o.reshape(bsz, s, DN_V).astype(h.dtype)

    return jnp.concatenate([y_a, y_b], axis=-1) @ w_out

def memory_cross_attention(h, m, w_q, w_k, w_v, w_o):
    bsz, s, _ = h.shape
    nm = m.shape[1]
    q = (h @ w_q).reshape(bsz, s, XA_HEADS, XA_DIM)
    k = (m @ w_k).reshape(bsz, nm, XA_HEADS, XA_DIM)
    v = (m @ w_v).reshape(bsz, nm, XA_HEADS, XA_DIM)
    scores = jnp.einsum('bshd,bmhd->bhsm', q, k).astype(jnp.float32) * (XA_DIM ** -0.5)
    p = jax.nn.softmax(scores, axis=-1).astype(v.dtype)
    o = jnp.einsum('bhsm,bmhd->bshd', p, v).reshape(bsz, s, D_MODEL)
    return o @ w_o

def squared_relu_mlp(h, w1, w2):
    return jnp.square(jax.nn.relu(h @ w1)) @ w2

def first_inputs(seed: int = 0) -> dict:
    key = jax.random.key(seed)
    ks = jax.random.split(key, 26)
    f32 = jnp.float32
    L = DEPTH

    def nrm(k, shape, scale):
        return jax.random.normal(k, shape, f32) * scale

    def gain(k, shape):
        return 1.0 + 0.02 * jax.random.normal(k, shape, f32)

    dt = jnp.exp(jax.random.uniform(ks[11], (L, DN_HEADS), f32, math.log(1e-3), math.log(1e-1)))
    return {
        "x": nrm(ks[0], (BATCH, SEQ, D_MODEL), 1.0),
        "mem": nrm(ks[1], (BATCH, N_MEM, D_MODEL), 1.0),
        "norm_mix": gain(ks[2], (L, D_MODEL)),
        "w_in": nrm(ks[3], (L, D_MODEL, D_IN), D_MODEL ** -0.5),
        "gm_ln_g": gain(ks[4], (L, GM_GROUPS, GM_DIM)),
        "gm_ln_b": nrm(ks[5], (L, GM_GROUPS, GM_DIM), 0.02),
        "gm_ws": nrm(ks[6], (L, GM_GROUPS, GM_CHUNK, GM_CHUNK), GM_CHUNK ** -0.5),
        "gm_bs": gain(ks[7], (L, GM_GROUPS, GM_CHUNK)),
        "dn_conv": nrm(ks[8], (L, CONV_W, 2 * DN_QK + DN_V), CONV_W ** -0.5),
        "dn_a_log": jnp.log(jax.random.uniform(ks[9], (L, DN_HEADS), f32, 1.0, 16.0)),
        "dn_dt_bias": dt + jnp.log(-jnp.expm1(-dt)),
        "dn_onorm": gain(ks[10], (L, DN_DV)),
        "w_out": nrm(ks[12], (L, MIX_WIDTH, D_MODEL), MIX_WIDTH ** -0.5),
        "norm_xa": gain(ks[13], (L, D_MODEL)),
        "norm_mem": gain(ks[14], (L, D_MODEL)),
        "xa_wq": nrm(ks[15], (L, D_MODEL, D_MODEL), D_MODEL ** -0.5),
        "xa_wk": nrm(ks[16], (L, D_MODEL, D_MODEL), D_MODEL ** -0.5),
        "xa_wv": nrm(ks[17], (L, D_MODEL, D_MODEL), D_MODEL ** -0.5),
        "xa_wo": nrm(ks[18], (L, D_MODEL, D_MODEL), D_MODEL ** -0.5),
        "norm_ffn": gain(ks[19], (L, D_MODEL)),
        "ffn_w1": nrm(ks[20], (L, D_MODEL, D_FF), D_MODEL ** -0.5),
        "ffn_w2": nrm(ks[21], (L, D_FF, D_MODEL), D_FF ** -0.5),
        "norm_final": gain(ks[22], (D_MODEL,)),
    }

def first_block(x, mem, norm_mix, w_in, gm_ln_g, gm_ln_b, gm_ws, gm_bs, dn_conv, dn_a_log, dn_dt_bias,
              dn_onorm, w_out, norm_xa, norm_mem, xa_wq, xa_wk, xa_wv, xa_wo, norm_ffn, ffn_w1, ffn_w2,
              norm_final):
    for l in range(DEPTH):
        h = rmsnorm(x, norm_mix[l])
        x = x + hybrid_mixer(h, w_in[l], gm_ln_g[l], gm_ln_b[l], gm_ws[l], gm_bs[l], dn_conv[l],
                             dn_a_log[l], dn_dt_bias[l], dn_onorm[l], w_out[l])
        m = rmsnorm(mem, norm_mem[l])
        x = x + memory_cross_attention(rmsnorm(x, norm_xa[l]), m, xa_wq[l], xa_wk[l], xa_wv[l], xa_wo[l])
        x = x + squared_relu_mlp(rmsnorm(x, norm_ffn[l]), ffn_w1[l], ffn_w2[l])
    return rmsnorm(x, norm_final)


CONV_WIDTH = D_MODEL
CONV_K = 3
HEAD_DIM = 64
N_Q_HEADS = 8
N_KV_HEADS = 2
GQA_GROUP = N_Q_HEADS // N_KV_HEADS
WINDOW = 128
BLOCK = WINDOW
ROPE_THETA = 10000.0
Q_WIDTH = N_Q_HEADS * HEAD_DIM
KV_WIDTH = N_KV_HEADS * HEAD_DIM
D_FF_2 = 2816
FFN_CONV_K = 3
EPS_2 = 1e-5

IN_SIZES_2 = (CONV_WIDTH, CONV_WIDTH, CONV_WIDTH, Q_WIDTH, KV_WIDTH, KV_WIDTH, D_MODEL, D_MODEL)
IN_WIDTH = sum(IN_SIZES_2)
IN_SPLITS = tuple(int(c) for c in np.cumsum(IN_SIZES_2)[:-1])


def rmsnorm_2(x, w):
    xf = x.astype(jnp.float32)
    xf = xf * lax.rsqrt(jnp.mean(xf * xf, axis=-1, keepdims=True) + EPS_2)
    return xf.astype(x.dtype) * w

def causal_dwconv_2(v, w, b=None):
    k_taps = w.shape[0]
    s = v.shape[1]
    vp = jnp.pad(v, ((0, 0), (k_taps - 1, 0), (0, 0)))
    y = sum(w[i] * vp[:, i:i + s] for i in range(k_taps))
    if b is not None:
        y = y + b
    return y

def rope_tables(positions, dtype):
    inv_freq = ROPE_THETA ** (-jnp.arange(0, HEAD_DIM, 2, dtype=jnp.float32) / HEAD_DIM)
    ang = positions.astype(jnp.float32)[..., None] * inv_freq
    return jnp.cos(ang)[:, :, None, :].astype(dtype), jnp.sin(ang)[:, :, None, :].astype(dtype)

def apply_rope(x, cos, sin):
    x1, x2 = jnp.split(x, 2, axis=-1)
    return jnp.concatenate([x1 * cos - x2 * sin, x2 * cos + x1 * sin], axis=-1)

def sliding_window_attention(q, k, v, sinks):
    b, s = q.shape[:2]
    nb = s // BLOCK
    qb = q.reshape(b, nb, BLOCK, N_KV_HEADS, GQA_GROUP, HEAD_DIM)

    def with_prev(t):
        tb = t.reshape(b, nb, BLOCK, N_KV_HEADS, HEAD_DIM)
        prev = jnp.pad(tb[:, :-1], ((0, 0), (1, 0), (0, 0), (0, 0), (0, 0)))
        return jnp.concatenate([prev, tb], axis=2)

    kk, vv = with_prev(k), with_prev(v)
    scale = HEAD_DIM ** -0.5
    scores = jnp.einsum('bnqhgd,bnkhd->bnhgqk', qb, kk).astype(jnp.float32) * scale

    q_pos = jnp.arange(BLOCK)[:, None] + BLOCK
    k_pos = jnp.arange(2 * BLOCK)[None, :]
    rel = q_pos - k_pos
    band = (rel >= 0) & (rel < WINDOW)
    not_pad = (jnp.arange(nb)[:, None, None] > 0) | (k_pos[None] >= BLOCK)
    valid = band[None] & not_pad
    scores = jnp.where(valid[None, :, None, None], scores, -jnp.inf)

    sink = sinks.astype(jnp.float32).reshape(N_KV_HEADS, GQA_GROUP)[None, None, :, :, None, None]
    m = jnp.maximum(jnp.max(scores, axis=-1, keepdims=True), sink)
    p = jnp.exp(scores - m)
    denom = jnp.sum(p, axis=-1, keepdims=True) + jnp.exp(sink - m)
    probs = (p / denom).astype(v.dtype)
    out = jnp.einsum('bnhgqk,bnkhd->bnqhgd', probs, vv)
    return out.reshape(b, s, Q_WIDTH)

def second_inputs(seed: int = 0) -> dict:
    key = jax.random.key(seed)
    ks = jax.random.split(key, 20)
    f32 = jnp.float32

    def nrm(k, shape, scale):
        return jax.random.normal(k, shape, f32) * scale

    x = jax.random.normal(ks[0], (BATCH, SEQ, D_MODEL), f32)
    positions = jnp.broadcast_to(jnp.arange(SEQ, dtype=jnp.int32), (BATCH, SEQ))
    return {
        "x": x,
        "positions": positions,
        "norm_mix_w": 1.0 + nrm(ks[1], (DEPTH, D_MODEL), 0.02),
        "w_in": nrm(ks[2], (DEPTH, D_MODEL, IN_WIDTH), D_MODEL ** -0.5),
        "b_in": nrm(ks[3], (DEPTH, IN_WIDTH), 0.02),
        "conv_mix_w": nrm(ks[4], (DEPTH, CONV_K, CONV_WIDTH), CONV_K ** -0.5),
        "w_conv_out": nrm(ks[5], (DEPTH, CONV_WIDTH, D_MODEL), CONV_WIDTH ** -0.5),
        "w_attn_out": nrm(ks[6], (DEPTH, Q_WIDTH, D_MODEL), Q_WIDTH ** -0.5),
        "b_attn_out": nrm(ks[7], (DEPTH, D_MODEL), 0.02),
        "sinks": nrm(ks[8], (DEPTH, N_Q_HEADS), 1.0),
        "w_mix_out": nrm(ks[9], (DEPTH, D_MODEL, D_MODEL), D_MODEL ** -0.5),
        "norm_ffn_w": 1.0 + nrm(ks[10], (DEPTH, D_MODEL), 0.02),
        "w_ffn_up": nrm(ks[11], (DEPTH, D_MODEL, 2 * D_FF_2), D_MODEL ** -0.5),
        "ffn_conv_w": nrm(ks[12], (DEPTH, FFN_CONV_K, D_FF_2), FFN_CONV_K ** -0.5),
        "ffn_conv_b": nrm(ks[13], (DEPTH, D_FF_2), 0.02),
        "w_ffn_down": nrm(ks[14], (DEPTH, D_FF_2, D_MODEL), D_FF_2 ** -0.5),
        "norm_final_w": 1.0 + nrm(ks[15], (D_MODEL,), 0.02),
    }

def second_block(x, positions, norm_mix_w, w_in, b_in, conv_mix_w, w_conv_out, w_attn_out,
              b_attn_out, sinks, w_mix_out, norm_ffn_w, w_ffn_up, ffn_conv_w, ffn_conv_b,
              w_ffn_down, norm_final_w):
    b, s, _ = x.shape
    cos, sin = rope_tables(positions, x.dtype)
    for l in range(DEPTH):
        u = rmsnorm_2(x, norm_mix_w[l])
        proj = u @ w_in[l] + b_in[l]
        cb, cc, cx, q, k, v, g_conv, g_attn = jnp.split(proj, IN_SPLITS, axis=-1)

        y_conv = (cb * causal_dwconv_2(cc * cx, conv_mix_w[l])) @ w_conv_out[l]

        q = apply_rope(q.reshape(b, s, N_Q_HEADS, HEAD_DIM), cos, sin)
        k = apply_rope(k.reshape(b, s, N_KV_HEADS, HEAD_DIM), cos, sin)
        v = v.reshape(b, s, N_KV_HEADS, HEAD_DIM)
        y_attn = sliding_window_attention(q, k, v, sinks[l]) @ w_attn_out[l] + b_attn_out[l]

        merged = jax.nn.sigmoid(g_conv) * y_conv + jax.nn.sigmoid(g_attn) * y_attn
        x = x + merged @ w_mix_out[l]

        u = rmsnorm_2(x, norm_ffn_w[l])
        up, gate = jnp.split(u @ w_ffn_up[l], 2, axis=-1)
        a = causal_dwconv_2(up, ffn_conv_w[l], ffn_conv_b[l])
        x = x + (jax.nn.silu(a) * gate) @ w_ffn_down[l]
    return rmsnorm_2(x, norm_final_w)


def setup_inputs(seed=0):
    out = dict(first_inputs(seed))
    for name, value in second_inputs(seed + 1).items():
        if name != "x":
            out[name + "_2"] = value
    return out


def reference(
    x, mem, norm_mix, w_in, gm_ln_g, gm_ln_b, gm_ws, gm_bs, dn_conv, dn_a_log, dn_dt_bias,
    dn_onorm, w_out, norm_xa, norm_mem, xa_wq, xa_wk, xa_wv, xa_wo, norm_ffn, ffn_w1, ffn_w2,
    norm_final, positions_2, norm_mix_w_2, w_in_2, b_in_2, conv_mix_w_2, w_conv_out_2,
    w_attn_out_2, b_attn_out_2, sinks_2, w_mix_out_2, norm_ffn_w_2, w_ffn_up_2, ffn_conv_w_2,
    ffn_conv_b_2, w_ffn_down_2, norm_final_w_2,
):
    x = first_block(
        x, mem, norm_mix, w_in, gm_ln_g, gm_ln_b, gm_ws, gm_bs, dn_conv, dn_a_log, dn_dt_bias,
        dn_onorm, w_out, norm_xa, norm_mem, xa_wq, xa_wk, xa_wv, xa_wo, norm_ffn, ffn_w1,
        ffn_w2, norm_final,
    )
    return second_block(
        x, positions_2, norm_mix_w_2, w_in_2, b_in_2, conv_mix_w_2, w_conv_out_2, w_attn_out_2,
        b_attn_out_2, sinks_2, w_mix_out_2, norm_ffn_w_2, w_ffn_up_2, ffn_conv_w_2,
        ffn_conv_b_2, w_ffn_down_2, norm_final_w_2,
    )


_drawn_inputs = setup_inputs


def setup_inputs(seed=0):
    import zlib

    import numpy as np

    out = dict(_drawn_inputs(seed))
    spreads = {}
    factors = {'gm_ln_g': 7.479,
     'gm_ln_b': 6.807,
     'gm_bs': 5.257,
     'dn_onorm': 5.26,
     'norm_xa': 8.0,
     'norm_mem': 8.0,
     'norm_mix_w_2': 2.923,
     'b_attn_out_2': 43.984,
     'sinks_2': 51.584,
     'norm_ffn_w_2': 13.571,
     'ffn_conv_b_2': 18.792,
     'norm_final_w_2': 8.255,
     'norm_ffn': 7.991,
     'b_in_2': 3.647}
    for name, (base, spread) in spreads.items():
        noise = np.random.default_rng([zlib.crc32(name.encode()), seed]).standard_normal(out[name].shape)
        drawn = base * np.exp(spread * noise) if base else spread * noise
        out[name] = __import__('jax').numpy.asarray(drawn.astype(out[name].dtype))
    for name, factor in factors.items():
        out[name] = (out[name] * factor).astype(out[name].dtype)
    return out
```

```python
from contextlib import ExitStack

import numpy as np

import concourse.bass as bass
from concourse import mybir

F32 = mybir.dt.float32
F32R = mybir.dt.float32r
I32 = mybir.dt.int32
ALU = mybir.AluOpType
ACT = mybir.ActivationFunctionType
AXIS_X = mybir.AxisListType.X

P = 128
D = 1024
KT = D // P
S = 512
NC = S // P
M = 256
MC = M // P
H = 4
XD = D // H
XT = XD // P
FF = 4 * D
FT = FF // P
F2T = 2816 // P
TAPS1, TAPS2 = 4, 3
PAD = TAPS1 - 1
EPS, EPS_2 = 1e-6, 1e-5
QH, KVH, HD = 8, 2, 64
QT = QH * HD // P
MASKED = -1e30

FFN_PARTS = [(k, min(k + KT, FT)) for k in range(0, FT, KT)]
FFN2_PARTS = [(k, min(k + KT, F2T)) for k in range(0, F2T, KT)]

UNITS_PER_BLOCK = 8
RAW_SLOTS = 4
SPLIT_SLOTS = 4
SPLIT_LEAD = SPLIT_SLOTS - 1


def weight_order():
    out = []

    def add(name, n, k0=0, k1=KT):
        out.append((name, n, k0, k1))

    for h in range(H):
        for part in range(3):
            add("qkv", part * H + h)
            if h == part == 0:
                add("logits", 0)
    for n in range(H):
        add("gu", n)
        add("gv", n)
    for n in range(H):
        add("gate", n)
    for n in range(KT):
        add("xa_wk", n)
    for n in range(KT):
        add("xa_wv", n)
    for n in range(KT):
        add("w_out", n)
    for n in range(KT):
        add("xa_wq", n)
    for n in range(KT):
        add("xa_wo", n)
    for k0, k1 in FFN_PARTS:
        for n in range(k0, k1):
            add("ffn_w1", n)
        for n in range(KT):
            add("ffn_w2", n, k0, k1)
    for n in range(QT):
        add("q2", n)
    add("k2", 0)
    add("v2", 0)
    for n in range(KT):
        add("cc2", n)
        add("cx2", n)
        add("cb2", n)
    for n in range(KT):
        add("gc2", n)
        add("conv_out2", n)
    for n in range(KT):
        add("ga2", n)
        add("attn_out2", n, 0, QT)
    for n in range(KT):
        add("mix2", n)
    for k0, k1 in FFN2_PARTS:
        for n in range(k0, k1):
            add("up2", n)
            add("gate2", n)
        for n in range(KT):
            add("down2", n, k0, k1)
    return out


WEIGHT_ORDER = weight_order()
N_UNITS = sum(k1 - k0 for _, _, k0, k1 in WEIGHT_ORDER)
N_BLOCKS = -(-N_UNITS // UNITS_PER_BLOCK)

COLUMNS = {}
for _name, _n in (("norm_mix", KT), ("norm_xa", KT), ("norm_mem", KT), ("norm_ffn", KT),
                  ("norm_final", KT), ("norm_mix2", KT), ("norm_ffn2", KT), ("norm_final2", KT),
                  ("dn_conv", TAPS1 * 3 * H), ("dn_onorm", 1), ("ln_g", H), ("ln_b", H),
                  ("b_cb", KT), ("b_cc", KT), ("b_cx", KT), ("b_q", QT), ("b_k", 1), ("b_v", 1),
                  ("b_gc", KT), ("b_ga", KT), ("conv_mix", TAPS2 * KT), ("b_attn_out", KT),
                  ("ffn_conv", TAPS2 * F2T), ("ffn_conv_b", F2T),
                  ("inv_freq", 1), ("minus_half", 1)):
    COLUMNS[_name] = (sum(n for _, n in COLUMNS.values()), _n)
N_COLUMNS = sum(n for _, n in COLUMNS.values())

ROWS = {}
for _name, _n in (("gm_bs", H * P), ("a_log", H), ("dt_bias", H)):
    ROWS[_name] = (sum(n for _, n in ROWS.values()), _n)
N_ROWS = sum(n for _, n in ROWS.values())

LEVELS = P.bit_length() - 1
EYE, ONES, UPPER, BOUND, ROTATE, BAND = 0, 1, 2, 3, 4, 5
LEVEL0 = 7
N_MATRICES = LEVEL0 + LEVELS


def constant_matrices():
    j, i = np.indices((P, P))
    rotate = np.where((j % HD >= HD // 2) & (i == j - HD // 2), -1.0, 0.0) + np.where(
        (j % HD < HD // 2) & (i == j + HD // 2), 1.0, 0.0)
    before = np.where(i > j, 0.0, MASKED)
    own = np.where(i <= j, 0.0, MASKED)
    out = [np.eye(P), np.ones((P, P)), j <= i, np.where(j <= i, 0.0, MASKED), rotate, before, own]
    for level in range(LEVELS):
        b = 1 << level
        out.append((i // (2 * b) == j // (2 * b)) & (i // b % 2 == 1) & (j // b % 2 == 0))
    return np.concatenate([np.asarray(m, np.float32) for m in out], axis=1)


class Counter:

    def __init__(self, handle):
        self.handle, self.value = handle, 0

    def add(self, n):
        self.value += n
        return (self, self.value)


def flat(marks):
    for m in marks:
        if isinstance(m, list):
            yield from flat(m)
        elif m:
            yield m


class Lane:

    def __init__(self, done):
        self.done, self.steps, self.seen = done, [], {}

    def wait(self, *marks):
        for counter, value in flat(marks):
            if value > self.seen.get(counter, 0):
                self.seen[counter] = value
                self.steps.append(lambda e, c=counter, v=value: e.wait_ge(c.handle, v))

    def run(self, make, after=(), signal=True, counter=None, by=1):
        self.wait(*after)
        if not signal:
            self.steps.append(make)
            return None
        counter = counter or self.done
        mark = counter.add(by)
        self.steps.append(lambda e: make(e).then_inc(counter.handle, by))
        return mark

    def play(self, engine):
        for step in self.steps:
            step(engine)


class Slot:
    def __init__(self, ap, wide):
        self.ap, self.wide, self.free, self.held = ap, wide, [], False

    def release(self, *marks):
        self.free, self.held = list(marks), False


class Ring:

    def __init__(self, aps, wide=None):
        self.slots, self.at = [Slot(a, w) for a, w in zip(aps, wide or aps)], 0

    def take(self):
        for _ in self.slots:
            slot = self.slots[self.at % len(self.slots)]
            self.at += 1
            if not slot.held:
                break
        assert not slot.held
        slot.held = True
        return slot


def over_tokens(ap, n):
    return ap.unsqueeze(1).broadcast_to([ap.shape[0], n, ap.shape[1]])


def along(ap, n):
    return ap.unsqueeze(2).broadcast_to([ap.shape[0], ap.shape[1], n])


def interleave(main, filler, main_steps, filler_steps):
    for i, _ in enumerate(main):
        if (i + 1) * filler_steps // main_steps > i * filler_steps // main_steps:
            next(filler, None)
    for _ in filler:
        pass


def build_program(nc, x_in, mem_in, weights_in, ws_in, columns_in, rows_in, sinks_in, matrices_in,
                  positions_in, out):
    with ExitStack() as base:
        def sbuf(name, shape, dtype=F32, stack=None):
            return (stack or base).enter_context(nc.sbuf_tensor(name, shape, dtype))

        def counter(name):
            return Counter(base.enter_context(nc.semaphore(name)))

        pe = Lane(counter("pe_done"))
        act = Lane(counter("act_done"))
        dve = Lane(counter("dve_done"))
        pool = Lane(counter("pool_done"))
        sync = Lane(counter("load_weights_issued"))
        raw_landed = [counter(f"raw_landed{i}") for i in range(RAW_SLOTS)]
        consts_landed = counter("consts_landed")
        x_landed = counter("x_landed")
        mem_landed = counter("mem_landed")
        pos_landed = counter("pos_landed")
        out_landed = counter("out_landed")

        raw = sbuf("w_raw", [P, RAW_SLOTS, UNITS_PER_BLOCK * P])
        w_hi = sbuf("w_hi", [P, SPLIT_SLOTS, UNITS_PER_BLOCK * P], F32R)
        w_lo = sbuf("w_lo", [P, SPLIT_SLOTS, UNITS_PER_BLOCK * P], F32R)
        a_hi = sbuf("a_hi", [P, KT, S], F32R)
        a_lo = sbuf("a_lo", [P, KT, S], F32R)
        columns = sbuf("columns", [P, N_COLUMNS])
        sinks = sbuf("sinks", [P, QH])
        matrices = sbuf("matrices", [P, N_MATRICES, P])
        rstd = sbuf("rstd", [P, S])
        square_sum = sbuf("square_sum", [P, S])
        squares = Ring([sbuf(f"square{i}", [P, S])[:, :] for i in range(2)])
        narrow = Ring([sbuf(f"narrow{i}", [P, H * NC])[:, :] for i in range(6)])
        wide = [sbuf(f"temp{i}", [P, PAD + S])[:, :] for i in range(5)]
        temps = Ring([w[:, PAD:] for w in wide], wide)
        banks = [base.enter_context(nc.psum_tensor(f"bank{i}", [P, S], F32)) for i in range(8)]
        proj_banks = Ring([b[:, :] for b in banks[:4]])
        side_banks = Ring([b[:, :] for b in banks[4:]])

        eye, ones, upper, bound, rotate = (matrices[:, i, :] for i in (EYE, ONES, UPPER, BOUND, ROTATE))

        def column(name, n=0):
            at, size = COLUMNS[name]
            assert n < size
            return columns[:, at + n:at + n + 1]

        def row(name, a=0, b=None):
            at, size = ROWS[name]
            return rows[:, at + a:at + (size if b is None else b)]

        def as_f32(ap):
            return ap.bitcast(F32)

        def matmul(to, lhs, rhs, start=True, stop=True, after=(), signal=True):
            return pe.run(lambda e: e.matmul(to, lhs, rhs, start=start, stop=stop), after, signal)

        def transpose(to, what, after=(), signal=True):
            n = what.shape[0]
            return pe.run(lambda e: e.transpose(to, what, matrices[0:n, EYE, 0:n]), after, signal)

        def activation(to, what, func, after=(), **kw):
            return act.run(lambda e: e.activation(to, what, func, **kw), after)

        def tensor_tensor(to, a, b, op, after=(), lane=None):
            return (lane or dve).run(lambda e: e.tensor_tensor(to, a, b, op), after)

        def tensor_scalar(to, a, s1, s2, op0, op1=None, after=(), lane=None):
            if op1 is None:
                return (lane or dve).run(lambda e: e.tensor_scalar(to, a, s1, None, op0), after)
            return (lane or dve).run(lambda e: e.tensor_scalar(to, a, s1, s2, op0, op1), after)

        def fused(to, a, s, b, op0, op1, after=()):
            return dve.run(lambda e: e.scalar_tensor_tensor(to, a, s, b, op0, op1), after)

        def copy(to, a, after=(), lane=None):
            return (lane or dve).run(lambda e: e.tensor_copy(to, a), after)

        def reciprocal(to, a, after=()):
            return dve.run(lambda e: e.reciprocal(to, a), after)

        def reduce_max(to, a, after=()):
            return dve.run(lambda e: e.reduce_max(to, a, AXIS_X), after)

        def mean_and_variance(to, stats, a, after=()):
            m = dve.run(lambda e: e.bn_stats(stats, a), after)
            return dve.run(lambda e: e.bn_aggr(to, stats), [m])

        def load(to, what, landed, after=(), lane=None):
            return (lane or sync).run(lambda e: e.dma_start(to, what), after, counter=landed, by=16)

        split_done, pe_done_with = {}, {}
        unit_at = [0]
        order = iter(WEIGHT_ORDER)

        def load_block(b):
            if b < N_BLOCKS:
                load(raw[:, b % RAW_SLOTS, :], weights_in[b], raw_landed[b % RAW_SLOTS],
                     after=split_done.get(b - RAW_SLOTS, ()))

        def split_block(b):
            r, s = b % RAW_SLOTS, b % SPLIT_SLOTS
            hi = activation(w_hi[:, s, :], raw[:, r, :], ACT.Copy,
                            after=[(raw_landed[r], 16 * (b // RAW_SLOTS + 1)), pe_done_with.get(b - SPLIT_SLOTS)])
            lo = tensor_tensor(w_lo[:, s, :], raw[:, r, :], as_f32(w_hi[:, s, :]), ALU.subtract,
                               after=[hi, pe_done_with.get(b - SPLIT_SLOTS)])
            split_done[b] = [hi, lo]
            load_block(b + RAW_SLOTS)

        def split_ahead(b):
            while len(split_done) < min(b + SPLIT_LEAD + 1, N_BLOCKS):
                following = len(split_done)
                if following >= SPLIT_SLOTS and following - SPLIT_SLOTS not in pe_done_with:
                    assert following > b
                    break
                split_block(following)

        class Projection:

            def __init__(self, name, n, hi, lo, ready, k0=0, k1=KT, width=S):
                assert next(order) == (name, n, k0, k1), (name, n, k0, k1)
                self.hi, self.lo, self.ready, self.k0, self.k1, self.width = hi, lo, ready, k0, k1, width
                self.bank, self.k, self.base = proj_banks.take(), k0, unit_at[0]
                unit_at[0] += k1 - k0

            def upto(self, k_end):
                to = self.bank.ap[:, 0:self.width]
                for k in range(self.k, k_end):
                    unit = self.base + k - self.k0
                    b, u = divmod(unit, UNITS_PER_BLOCK)
                    split_ahead(b)
                    cols = slice(u * P, (u + 1) * P)
                    wh, wl = w_hi[:, b % SPLIT_SLOTS, cols], w_lo[:, b % SPLIT_SLOTS, cols]
                    units_left[b] = units_left.get(b, min(UNITS_PER_BLOCK, N_UNITS - b * UNITS_PER_BLOCK)) - 1
                    matmul(to, wh, self.hi(k), k == self.k0, False, [split_done[b], self.ready(k), self.bank.free], signal=False)
                    matmul(to, wh, self.lo(k), False, False, signal=False)
                    last = k == self.k1 - 1
                    done = matmul(to, wl, self.hi(k), False, last, signal=last or not units_left[b])
                    if not units_left[b]:
                        pe_done_with[b] = done
                    if last:
                        self.done = done
                self.k = k_end
                return self.bank, (self.done if k_end == self.k1 else None)

        units_left, begun = {}, {}

        def project(*args, **kw):
            if args[:2] in begun:
                return begun.pop(args[:2])
            it = Projection(*args, **kw)
            return it.upto(it.k1)

        def begin_between(tiles, steps):
            for (name, n), step in zip(tiles, steps):
                begun[name, n] = Projection(name, n, *a_parts()).upto(KT)
                step()

        def finish():
            for n in range(KT):
                stored = load(out[n], xs[:, n, :], out_landed, after=[x_ready[n]])
            sync.wait(stored)
            block = base.enter_context(nc.Block())
            block.sync(sync.play)
            block.tensor(pe.play)
            block.scalar(act.play)
            block.vector(dve.play)
            block.gpsimd(pool.play)

        gain12 = sbuf("gain12", [P, KT])
        x_first = ExitStack()
        x0 = sbuf("x_first", [P, KT, S], stack=x_first)
        x_first.close()
        delta = ExitStack()
        qk_t = sbuf("qk_t", [P, H, NC, P], stack=delta)
        y_a = sbuf("y_a", [P, H, S], stack=delta)
        qkv = sbuf("qkv", [P, 3 * H, S], stack=delta)
        k_dec = sbuf("k_dec", [P, H, NC, P], stack=delta)
        inv = [sbuf(f"inv{i}", [P, NC, P], stack=delta) for i in range(2)]
        inv_t = [sbuf(f"inv_t{i}", [P, NC, P], stack=delta) for i in range(2)]
        level_y = [sbuf(f"level_y{i}", [P, NC, P], stack=delta) for i in range(2)]
        strict_t = [sbuf(f"strict_t{i}", [P, NC, P], stack=delta) for i in range(2)]
        level_b = [[sbuf(f"level_b{i}{j}", [P, NC, P], stack=delta) for j in range(2)] for i in range(2)]
        gate = sbuf("gate", [P, H, S], stack=delta)
        rows = sbuf("rows", [P, N_ROWS], stack=delta)
        ws = sbuf("ws", [P, H, P], stack=delta)
        mix_bias = sbuf("mix_bias", [P, H, P], stack=delta)
        small = sbuf("small", [P, 12, H * NC], stack=delta)
        ln_stats = [sbuf(f"ln_stats{i}", [P, NC, 6], stack=delta) for i in range(2)]
        ln_mean = [sbuf(f"ln_mean{i}", [P, NC, 2], stack=delta) for i in range(2)]
        mem_x = sbuf("mem_x", [P, KT, M], stack=delta)
        mem_rstd = sbuf("mem_rstd", [P, M], stack=delta)
        delta.close()
        xs = sbuf("xs", [P, KT, S])
        b_hi = sbuf("b_hi", [P, KT, S], F32R)
        b_lo = sbuf("b_lo", [P, KT, S], F32R)
        cross = ExitStack()
        mem_k = sbuf("mem_k", [P, KT, M], stack=cross)
        mem_v = sbuf("mem_v", [P, MC, D], stack=cross)
        recur = ExitStack()
        memory_s = sbuf("memory_s", [P, H, P], stack=recur)
        memory_d = sbuf("memory_d", [P, H, P], stack=recur)
        v_new = sbuf("v_new", [P, H, P], stack=recur)
        recur.close()
        m_hi, m_lo = (a[:, 0:KT // 2, :].rearrange("p t (h m) -> p (t h) m", m=M) for a in (a_hi, a_lo))
        columns_landed = counter("columns_landed")
        first_matrices_landed = counter("first_matrices_landed")
        x_tile_landed = [counter(f"x_tile_landed{t}") for t in range(KT)]
        FIRST_MATRICES = ROTATE
        m_in = matrices_in.rearrange("p (m c) -> p m c", c=P)
        load(columns[:, :], columns_in, columns_landed)
        load_block(0)
        x_first_ready = []
        for t in range(KT):
            x_first_ready.append(load(x0[:, t, :], x_in[t], x_tile_landed[t], lane=act if t in (0, 2) else sync))
            if t == KT // 2:
                load_block(1)
        load_block(2)
        load_block(3)
        first_consts = load(matrices[:, 0:FIRST_MATRICES, :], m_in[:, 0:FIRST_MATRICES, :], first_matrices_landed, lane=pool)
        load(rows[:, :], rows_in.partition_broadcast(P), consts_landed, lane=pool)
        load(matrices[:, FIRST_MATRICES:, :], m_in[:, FIRST_MATRICES:, :], consts_landed, lane=pool)
        load(sinks[:, :], sinks_in.partition_broadcast(P), consts_landed, lane=pool)
        consts = load(ws[:, :, :], ws_in, consts_landed, lane=pool)
        mem_ready = load(mem_x[:, :, :], mem_in, mem_landed, lane=pool)

        state = {"rstd_read": [], "sum_read": [], "sum2_read": [], "a_read": []}

        def stage_input(x, gain, after, hi, lo):
            h = activation(hi, x, ACT.Copy, after=[after, state["a_read"]], scale=gain)
            low = fused(lo, x, gain, as_f32(hi), ALU.mult, ALU.subtract, after=[after, h])
            return [h, low]

        def stage_square(t, x, after, total, scale=1.0, key="sum", lane=None):
            if t == 0:
                state[key] = activation(total, x, ACT.Square, after=[after, state[key + "_read"]], scale=scale)
            else:
                sq = squares.take()
                to = sq.ap[:, 0:total.shape[1]]
                m = activation(to, x, ACT.Square, after=[after, sq.free], scale=scale)
                state[key] = tensor_tensor(total, total, to, ALU.add, after=[m, state[key]], lane=lane or pool)
                sq.release(state[key])
            return state[key]

        def token_sums(ap, summed, chunks=NC):
            bank = side_banks.take()
            for c in range(chunks):
                t = matmul(bank.ap[:, c:c + 1], ap[:, c * P:(c + 1) * P], ones[:, 0:1],
                           after=[summed, first_consts, bank.free], signal=(c == chunks - 1))
            return bank, t

        def power(ap, after):
            return tensor_tensor(ap, ap, column("minus_half").broadcast_to([P, ap.shape[1]]), ALU.pow,
                                 after=[after, first_consts], lane=pool)

        def token_root(ap, summed, scale, eps, chunks=NC):
            bank, t = token_sums(ap, summed, chunks)
            slot = narrow.take()
            to = slot.ap[:, 0:chunks]
            m = tensor_scalar(to, bank.ap[:, 0:chunks], scale, eps, ALU.mult, ALU.add, after=[t, slot.free])
            bank.release(m)
            return slot, power(to, m), t

        def spread(narrow_ap, ready, chunks=NC):
            bank = side_banks.take()
            for c in range(chunks):
                t = matmul(bank.ap[:, c * P:(c + 1) * P], narrow_ap[:, c:c + 1].broadcast_to([P, P]), eye,
                           after=[ready, bank.free], signal=(c == chunks - 1))
            return bank, t

        def spread_to(to, slot, ready, to_free, chunks=NC):
            bank, t = spread(slot.ap, ready, chunks)
            slot.release(t)
            done = activation(to, bank.ap[:, 0:chunks * P], ACT.Copy, after=[t, to_free])
            bank.release(done)
            return done

        def leave(bank, done, to, to_free=(), n=S, scale=None, ready=None):
            m = tensor_tensor(to, bank.ap[:, 0:n], (rstd if scale is None else scale)[:, 0:n], ALU.mult,
                              after=[done, (state["rstd"] if ready is None else ready), to_free])
            bank.release(m)
            if scale is None:
                state["rstd_read"] = [m]
            return m

        def rstd_steps(eps):
            part = []

            def root():
                slot, r, t = token_root(square_sum[:, :], state["sum"], 1.0 / D, eps)
                state["sum_read"] = [t]
                part.extend([slot, r])

            def to_row():
                state["rstd"] = spread_to(rstd[:, :], *part, state["rstd_read"])

            return root, to_row

        a_ready = {}
        for lane in (act, dve, pool):
            lane.wait((columns_landed, 16))
        split_block(0)
        for t in range(KT):
            a_ready[t] = stage_input(x0[:, t, :], column("norm_mix", t), x_first_ready[t], a_hi[:, t, :], a_lo[:, t, :])
        split_block(1)
        for t in range(KT):
            stage_square(t, x0[:, t, :], x_first_ready[t], square_sum[:, :])
            if t == KT // 2:
                split_block(2)
        x0_read = [state["sum"], a_ready[KT - 1]]

        def a_parts():
            return (lambda k: a_hi[:, k, :]), (lambda k: a_lo[:, k, :]), (lambda k, r=dict(a_ready): r[k])

        ws_ready = pool.run(lambda e: e.affine_select(
            out=ws[:, :, :], in_=ws[:, :, :], pattern=[[0, H], [1, P]], compare_op=ALU.is_ge, fill=0.0,
            base=0, channel_multiplier=-1), after=[consts])

        hi, lo, ready = a_parts()

        def gates():
            bank, done = project("logits", 0, hi, lo, ready)
            yield
            first = temps.take()
            m = tensor_tensor(first.ap[0:2 * H, :], bank.ap[0:2 * H, :], rstd[0:2 * H, :], ALU.mult,
                              after=[done, state["rstd"], first.free])
            bank.release(m)
            yield
            bank = side_banks.take()
            logits = bank.ap[:, 0:NC * 2 * H].rearrange("p (c n) -> p c n", c=NC)
            for c in range(NC):
                t = transpose(logits[:, c, :], first.ap[0:2 * H, c * P:(c + 1) * P], after=[m, bank.free, first_consts])
            first.release(t)
            (BETA, A_IN, NEG_ABS, SOFT, G, CUM, TOTAL, CUM_EXP, K_SCALE, TOTAL_EXP, B_CUM, RATE) = (
                small[:, i, :] for i in range(12))

            def by_chunk(ap):
                return ap.rearrange("p (h c) -> p c h", h=H)

            m2 = tensor_tensor(by_chunk(A_IN), logits[:, :, H:2 * H], over_tokens(row("dt_bias"), NC), ALU.add, after=[t, consts])
            e1 = activation(by_chunk(BETA), logits[:, :, 0:H], ACT.Exp, after=[m2], scale=-1.0)
            bank.release(e1)
            d1 = tensor_scalar(BETA, BETA, 1.0, None, ALU.add, after=[e1])
            d1 = reciprocal(BETA, BETA, after=[d1])
            n1 = tensor_scalar(NEG_ABS, A_IN, -1.0, None, ALU.mult, after=[m2])
            n1 = tensor_tensor(NEG_ABS, NEG_ABS, A_IN, ALU.min, after=[n1])
            e2 = activation(SOFT, NEG_ABS, ACT.Exp, after=[n1])
            e3 = activation(RATE[:, 0:H], row("a_log"), ACT.Exp, after=[consts])
            e2 = activation(SOFT, SOFT, ACT.Ln, after=[e2], bias=1.0)
            s1 = fused(SOFT, A_IN, 0.0, SOFT, ALU.max, ALU.add, after=[e2])
            g = fused(G.rearrange("p (h c) -> p h c", h=H), SOFT.rearrange("p (h c) -> p h c", h=H), -1.0,
                      along(RATE[:, 0:H], NC), ALU.mult, ALU.mult, after=[s1, e3])
            yield
            bank = side_banks.take()
            matmul(bank.ap[:, 0:H * NC], upper, G, after=[g, bank.free], signal=False)
            t = matmul(bank.ap[:, 16:16 + H * NC], ones, G)
            c1 = copy(small[:, 5:7, :], bank.ap[:, 0:2 * H * NC].rearrange("p (a n) -> p a n", a=2), after=[t])
            bank.release(c1)
            k1 = tensor_tensor(K_SCALE, TOTAL, CUM, ALU.subtract, after=[c1])
            e4 = activation(CUM_EXP, CUM, ACT.Exp, after=[c1])
            e5 = activation(TOTAL_EXP, TOTAL, ACT.Exp)
            e6 = activation(K_SCALE, K_SCALE, ACT.Exp, after=[k1])
            b1 = tensor_tensor(B_CUM, BETA, CUM_EXP, ALU.mult, after=[e4, d1])
            state["small"] = [b1, e6, e5, g]
            yield
            bank = side_banks.take()
            t = matmul(bank.ap, ones, ws[:, :, :].rearrange("p h t -> p (h t)"), after=[ws_ready, bank.free])
            for n in range(H):
                m = fused(mix_bias[:, n, :], bank.ap[:, n * P:(n + 1) * P], column("ln_b", n),
                          row("gm_bs", n * P, (n + 1) * P), ALU.mult, ALU.add, after=[t])
            bank.release(m)
            state["mix_bias"] = m
            yield

        BETA, G, CUM, K_SCALE, TOTAL_EXP, B_CUM = (small[:, i, :] for i in (0, 4, 5, 8, 9, 10))

        qkv_ready = {}

        def causal_conv(buf, ready, acc, taps, weight):
            z = dve.run(lambda e: e.memset(buf.wide[:, 0:PAD], 0.0), after=[buf.free])
            tap = [buf.wide[:, PAD - (taps - 1) + i:PAD - (taps - 1) + i + S] for i in range(taps)]
            y = activation(acc.ap, tap[-1], ACT.Copy, after=[ready, acc.free], scale=weight(taps - 1))
            for i in range(taps - 1):
                y = fused(acc.ap, tap[i], weight(i), acc.ap, ALU.mult, ALU.add, after=[y, z])
            buf.release(y)
            return y

        aside, convolved, squared = [], [], {}

        def halves_and_aside(name, n):
            it = Projection(name, n, hi, lo, ready)
            it.upto(KT // 2)
            while convolved:
                convolved.pop(0)()
            if aside:
                aside.pop(0)()
            yield
            bank, done = it.upto(KT)
            if aside:
                aside.pop(0)()
            return bank, done

        def conv_qkv(n):
            bank, done = yield from halves_and_aside("qkv", n)
            if n in (0, H):
                yield
            buf = temps.take()
            m = leave(bank, done, buf.ap, buf.free)
            acc = temps.take()
            y = causal_conv(buf, m, acc, TAPS1, lambda i: column("dn_conv", i * 3 * H + n))

            def shape():
                qkv_ready[n] = activation(qkv[:, n, :], acc.ap, ACT.Silu, after=[y])
                acc.release(qkv_ready[n])
                if n < 2 * H:
                    sq = squares.take()
                    squared[n] = sq, activation(sq.ap, qkv[:, n, :], ACT.Square, after=[qkv_ready[n], sq.free])

            convolved.append(shape)
            yield

        def unit_norms(h):
            slot, norm_bank, parts = [], [], (h, H + h)

            def sums():
                bank = side_banks.take()
                for i, n in enumerate(parts):
                    sq, m = squared[n]
                    for c in range(NC):
                        t = matmul(bank.ap[:, i * NC + c:i * NC + c + 1], sq.ap[:, c * P:(c + 1) * P], ones[:, 0:1],
                                   after=[m, bank.free])
                    sq.release(t)
                both = narrow.take()
                m = tensor_scalar(both.ap[:, 0:2 * NC], bank.ap[:, 0:2 * NC], EPS, None, ALU.add, after=[t, both.free])
                bank.release(m)
                slot.append((both, power(both.ap[:, 0:2 * NC], m)))

            def scales():
                both, r = slot[0]
                for i, n in enumerate(parts):
                    bank, t = spread(both.ap[:, i * NC:(i + 1) * NC], r)
                    qkv_ready[n] = fused(qkv[:, n, :], qkv[:, n, :], (P ** -0.5, 1.0)[i], bank.ap, ALU.mult, ALU.mult, after=[t])
                    bank.release(qkv_ready[n])
                both.release(t)
                heads_projected.append(h)

            return [sums, scales]

        def keep_gate(n):
            bank, done = yield from halves_and_aside("gate", n)
            state["a_read"] = [done]
            m = leave(bank, done, gate[:, n, :])
            gate_ready[n] = activation(gate[:, n, :], gate[:, n, :], ACT.Silu, after=[m])
            yield

        gate_ready, y_a_ready, b_ready, x_read = {}, {}, {}, {}

        def spatial(n):
            bank, done = yield from halves_and_aside("gu", n)
            m = leave(bank, done, y_a[:, n, :], x0_read)
            u = activation(y_a[:, n, :], y_a[:, n, :], ACT.Gelu_apprx_tanh, after=[m])
            yield
            bank, done = yield from halves_and_aside("gv", n)
            v = temps.take()
            m = leave(bank, done, v.ap, v.free)
            gelu = activation(v.ap, v.ap, ACT.Gelu_apprx_tanh, after=[m])
            rest = {}

            def statistics():
                bank = side_banks.take()
                for c in range(NC):
                    t = transpose(bank.ap[:, c * P:(c + 1) * P], v.ap[:, c * P:(c + 1) * P], after=[gelu, bank.free])
                v.release(t)
                stats, mean_var = ln_stats[n % 2], ln_mean[n % 2]
                for c in range(NC):
                    a = mean_and_variance(mean_var[:, c, :], stats[:, c, :], bank.ap[:, c * P:(c + 1) * P],
                                          after=[t, ln_free.get(n - 2)])
                i1 = tensor_scalar(mean_var[:, :, 1], mean_var[:, :, 1], EPS, None, ALU.add, after=[a])
                rest["rstd"], rest["bank"] = power(mean_var[:, :, 1], i1), bank

            def normalise():
                bank, mean_var, normed = rest["bank"], ln_mean[n % 2], temps.take()
                for c in range(NC):
                    at = slice(c * P, (c + 1) * P)
                    w = tensor_scalar(normed.ap[:, at], bank.ap[:, at], mean_var[:, c, 0:1], mean_var[:, c, 1:2],
                                      ALU.subtract, ALU.mult, after=[rest["rstd"], normed.free])
                bank.release(w)
                ln_free[n] = w
                rest["normed"], rest["ready"] = normed, w

            def mix():
                bank, normed = side_banks.take(), rest["normed"]
                for c in range(NC):
                    at = slice(c * P, (c + 1) * P)
                    t = matmul(bank.ap[:, at], normed.ap[:, at], ws[:, n, :], after=[rest["ready"], ws_ready, bank.free])
                m = fused(chunked(normed.ap), chunked(bank.ap), column("ln_g", n), over_tokens(mix_bias[:, n, :], NC),
                          ALU.mult, ALU.add, after=[t, state["mix_bias"]])
                bank.release(m)
                y_a_ready[n] = tensor_tensor(y_a[:, n, :], y_a[:, n, :], normed.ap, ALU.mult, after=[m, u])
                normed.release(y_a_ready[n])

            aside.extend([statistics, normalise, mix])
            yield

        ln_free = {}

        def chunked(ap):
            return ap.rearrange("p (c d) -> p c d", c=NC)

        head_done = {}

        def delta_head(h):
            q, k, v = (chunked(qkv[:, i * H + h, :]) for i in range(3))
            q_ready, k_ready, v_ready = (qkv_ready[i * H + h] for i in range(3))
            i = h % 2
            before = head_done.get(h - 2)
            cols = slice(h * NC, (h + 1) * NC)
            rows_bank = side_banks.take()
            for c in range(NC):
                at = slice(c * P, (c + 1) * P)
                col = h * NC + c
                t = matmul(rows_bank.ap[:, at], G[:, col:col + 1].broadcast_to([P, P]), upper,
                           after=[state["small"], rows_bank.free])
            cum = temps.take()
            row_exp = activation(cum.ap, rows_bank.ap, ACT.Exp, after=[t, cum.free])
            decay = level_y[i]
            m = tensor_tensor(decay[:, :, :], chunked(rows_bank.ap), along(CUM[:, cols], P), ALU.subtract, after=[row_exp, before])
            rows_bank.release(m)
            m = tensor_tensor(decay[:, :, :], decay[:, :, :], over_tokens(bound, NC), ALU.min, after=[m, first_consts])
            decayed = activation(decay[:, :, :], decay[:, :, :], ACT.Exp, after=[m])
            yield
            kk_bank, qk_bank = side_banks.take(), side_banks.take()
            for c in range(NC):
                at = slice(c * P, (c + 1) * P)
                matmul(kk_bank.ap[:, at], k[:, c, :], k[:, c, :], after=[k_ready, kk_bank.free], signal=False)
                t = matmul(qk_bank.ap[:, at], k[:, c, :], q[:, c, :], after=[q_ready, qk_bank.free])
            beta_bank = side_banks.take()
            for c in range(NC):
                col = h * NC + c
                beta = matmul(beta_bank.ap[:, c * P:(c + 1) * P], BETA[:, col:col + 1].broadcast_to([P, P]), eye,
                              after=[beta_bank.free])
            st = strict_t[i]
            m = tensor_tensor(st[:, :, :], chunked(kk_bank.ap), decay[:, :, :], ALU.mult, after=[t, decayed])
            kk_bank.release(m)
            strict = tensor_tensor(st[:, :, :], st[:, :, :], chunked(beta_bank.ap), ALU.mult, after=[m, beta])
            beta_bank.release(strict)

            def level_mask(level, after, lane=None):
                return tensor_tensor(level_b[i][level % 2][:, :, :], st[:, :, :],
                                     over_tokens(matrices[:, LEVEL0 + level, :], NC), ALU.mult, after=after, lane=lane or pool)

            x, x_t, y = inv[i], inv_t[i], level_y[i]
            mask = level_mask(0, [strict, before, consts], lane=dve)
            xt_ok = tensor_tensor(x_t[:, :, :], over_tokens(eye, NC), level_b[i][0][:, :, :], ALU.subtract, after=[mask])
            mask = level_mask(1, [strict, before])
            qk = tensor_tensor(qk_t[:, h, :, :], chunked(qk_bank.ap), decay[:, :, :], ALU.mult, after=[x0_read])
            qk_bank.release(qk)
            q_dec = tensor_tensor(q, q, chunked(cum.ap), ALU.mult, after=[row_exp, t, q_ready], lane=pool)
            cum.release(q_dec)
            yield
            bank = side_banks.take()
            for c in range(NC):
                t = transpose(bank.ap[:, c * P:(c + 1) * P], x_t[:, c, :], after=[xt_ok, bank.free])
            x_ok = copy(x[:, :, :], chunked(bank.ap), after=[t])
            bank.release(x_ok)
            b_read = [xt_ok]
            yield
            for level in range(1, LEVELS):
                last = level == LEVELS - 1
                b, b_ok = level_b[i][level % 2], mask
                if not last:
                    mask = level_mask(level + 1, [b_read])
                bank = side_banks.take()
                for c in range(NC):
                    t = matmul(bank.ap[:, c * P:(c + 1) * P], b[:, c, :], x[:, c, :], after=[b_ok, x_ok, bank.free])
                b_read = [t]
                y_ok = activation(y[:, :, :], chunked(bank.ap), ACT.Copy, after=[t, qk])
                bank.release(y_ok)
                if last:
                    k_bank, v_bank = side_banks.take(), side_banks.take()
                    kb_t, vb_t = st, level_b[i][(level - 1) % 2]
                    for c in range(NC):
                        at = slice(c * P, (c + 1) * P)
                        transpose(k_bank.ap[:, at], k[:, c, :], after=[k_bank.free], signal=False)
                        t = transpose(v_bank.ap[:, at], v[:, c, :], after=[v_ready, v_bank.free])
                    kb = tensor_tensor(kb_t[:, :, :], chunked(k_bank.ap), along(B_CUM[:, cols], P), ALU.mult, after=[t, b_ok])
                    vb = tensor_tensor(vb_t[:, :, :], chunked(v_bank.ap), along(BETA[:, cols], P), ALU.mult, after=[b_read])
                    v_bank.release(vb)
                    kd = tensor_tensor(k_dec[:, h, :, :], chunked(k_bank.ap), along(K_SCALE[:, cols], P), ALU.mult)
                    k_bank.release(kd)
                yield
                bank_t = side_banks.take()
                for c in range(NC):
                    t = matmul(bank_t.ap[:, c * P:(c + 1) * P], y[:, c, :], x_t[:, c, :], after=[y_ok, xt_ok, bank_t.free])
                if not last:
                    bank = side_banks.take()
                    for c in range(NC):
                        t = matmul(bank.ap[:, c * P:(c + 1) * P], x_t[:, c, :], y[:, c, :], after=[bank.free])
                    x_ok = tensor_tensor(x[:, :, :], x[:, :, :], chunked(bank.ap), ALU.subtract, after=[t])
                    bank.release(x_ok)
                xt_ok = tensor_tensor(x_t[:, :, :], x_t[:, :, :], chunked(bank_t.ap), ALU.subtract, after=[t])
                bank_t.release(xt_ok)
                yield
            w_bank, u_bank = side_banks.take(), side_banks.take()
            for c in range(NC):
                at = slice(c * P, (c + 1) * P)
                matmul(w_bank.ap[:, at], kb_t[:, c, :], x_t[:, c, :], after=[kb, xt_ok, w_bank.free], signal=False)
                t = matmul(u_bank.ap[:, at], x_t[:, c, :], vb_t[:, c, :], after=[vb, u_bank.free])
            w = activation(k, chunked(w_bank.ap), ACT.Copy, after=[t])
            w_bank.release(w)
            u = activation(v, chunked(u_bank.ap), ACT.Copy)
            u_bank.release(u)
            head_done[h] = [t, vb, kd, q_dec, qk, w, u]
            yield

        def recurrence():
            q_dec, w_t, u = (qkv[:, i * H:(i + 1) * H, :].rearrange("p h (c d) -> p h c d", c=NC) for i in range(3))
            all_heads = [head_done[h] for h in range(H)]
            s_ok = None

            def heads(ap):
                return ap.rearrange("p (h d) -> p h d", h=H)

            total = TOTAL_EXP.rearrange("p (h c) -> p h c", h=H)
            o_read = None
            for c in range(NC):
                if c == 0:
                    new = copy(v_new[:, :, :], u[:, :, 0, :], after=[all_heads])
                else:
                    bank = side_banks.take()
                    for h in range(H):
                        t = matmul(heads(bank.ap)[:, h, :], w_t[:, h, c, :], memory_s[:, h, :], after=[s_ok, bank.free])
                    new = tensor_tensor(v_new[:, :, :], u[:, :, c, :], heads(bank.ap), ALU.subtract, after=[t, v_read])
                    bank.release(new)
                    yield
                if c < NC - 1:
                    bank = side_banks.take()
                    for h in range(H):
                        t = matmul(heads(bank.ap)[:, h, :], k_dec[:, h, c, :], v_new[:, h, :], after=[new, bank.free])
                    if c == 0:
                        s_next = copy(memory_s[:, :, :], heads(bank.ap), after=[t])
                    o_bank = side_banks.take()
                    for h in range(H):
                        if c:
                            matmul(heads(o_bank.ap)[:, h, :], memory_s[:, h, :], q_dec[:, h, c, :], True, False,
                                   after=[o_bank.free], signal=False)
                        o = matmul(heads(o_bank.ap)[:, h, :], v_new[:, h, :], qk_t[:, h, c, :], c == 0, True,
                                   after=[new, o_bank.free])
                    if c:
                        s_next = tensor_tensor(memory_s[:, :, :], memory_d[:, :, :], heads(bank.ap), ALU.add, after=[o, decayed])
                    bank.release(s_next)
                    if c + 1 < NC - 1:
                        decayed = tensor_tensor(memory_d[:, :, :], memory_s[:, :, :], along(total[:, :, c + 1], P), ALU.mult,
                                                after=[s_next], lane=pool)
                    s_ok = s_next
                else:
                    o_bank = side_banks.take()
                    for h in range(H):
                        matmul(heads(o_bank.ap)[:, h, :], memory_s[:, h, :], q_dec[:, h, c, :], True, False,
                               after=[o_bank.free], signal=False)
                        o = matmul(heads(o_bank.ap)[:, h, :], v_new[:, h, :], qk_t[:, h, c, :], False, True, after=[new])
                v_read = [o]
                o_read = activation(qk_t[:, :, c, :], heads(o_bank.ap), ACT.Copy, after=[o])
                o_bank.release(o_read)
                yield
            state["o"] = o_read

        def head_outputs():
            o = [qk_t[:, h, :, :].rearrange("p c t -> p (c t)") for h in range(H)]
            bank = side_banks.take()
            roots = narrow.take()
            for h in range(H):
                sq = squares.take()
                m = activation(sq.ap, o[h], ACT.Square, after=[state["o"], sq.free])
                for c in range(NC):
                    t = matmul(bank.ap[:, h * NC + c:h * NC + c + 1], sq.ap[:, c * P:(c + 1) * P], ones[:, 0:1],
                               after=[m, bank.free])
                sq.release(t)
                if h % 2:
                    yield
            m = tensor_scalar(roots.ap, bank.ap[:, 0:H * NC], 1.0 / P, EPS, ALU.mult, ALU.add, after=[t, roots.free])
            bank.release(m)
            r = power(roots.ap, m)
            for h in range(H):
                split_to_b(h, y_a[:, h, :], [y_a_ready[h]], lane=pool)
            yield
            for h in range(H):
                bank, t = spread(roots.ap[:, h * NC:(h + 1) * NC], r)
                out_t = temps.take()
                m = fused(out_t.ap, o[h], column("dn_onorm"), bank.ap, ALU.mult, ALU.mult, after=[t, out_t.free])
                bank.release(m)
                y = tensor_tensor(gate[:, h, :], gate[:, h, :], out_t.ap, ALU.mult, after=[m, gate_ready[h]])
                out_t.release(y)
                gate_ready[h] = y
                if h:
                    split_to_b(H + h - 1, gate[:, h - 1, :], gate_ready[h - 1])
                yield
            split_to_b(2 * H - 1, gate[:, H - 1, :], gate_ready[H - 1])
            roots.release(t)

        def split_parts(x, hi, lo, after, lane=None):
            h = activation(hi, x, ACT.Copy, after=[after])
            return [h, tensor_tensor(lo, x, as_f32(hi), ALU.subtract, after=[h, after], lane=lane)]

        def split_to_b(n, x, after, lane=None):
            b_ready[n] = split_parts(x, b_hi[:, n, :], b_lo[:, n, :], [after, state.get("b_read")], lane)
            return b_ready[n]

        def b_parts(at=lambda k: k):
            marks = dict(b_ready)
            return (lambda k: b_hi[:, at(k), :]), (lambda k: b_lo[:, at(k), :]), (lambda k: marks[at(k)])

        def memory_norm():
            total = temps.take()
            state["mem_sum_read"] = total.free
            for t in range(KT):
                stage_square(t, mem_x[:, t, :], mem_ready, total.ap[:, 0:M], key="mem_sum")
            yield
            slot, r, t = token_root(total.ap, state["mem_sum"], 1.0 / D, EPS, MC)
            total.release(t)
            yield
            state["mem_scale"] = spread_to(mem_rstd[:, :], slot, r, [], MC)

        def memory_keys_and_values():
            m_ready = {}
            for t in range(KT):
                m_ready[t] = stage_input(mem_x[:, t, :], column("norm_mem", t), mem_ready, m_hi[:, t, :], m_lo[:, t, :])
            hi, lo, ready = (lambda k: m_hi[:, k, :]), (lambda k: m_lo[:, k, :]), (lambda k: m_ready[k])
            yield
            for n in range(KT):
                bank, done = project("xa_wk", n, hi, lo, ready, width=M)
                state["mem_k"] = leave(bank, done, mem_k[:, n, :], [head_done[h] for h in range(H)], n=M, scale=mem_rstd, ready=state["mem_scale"])
                yield
            for n in range(KT):
                bank, done = project("xa_wv", n, hi, lo, ready, width=M)
                v = temps.take()
                m = leave(bank, done, v.ap[:, 0:M], v.free, n=M, scale=mem_rstd, ready=state["mem_scale"])
                yield
                bank = side_banks.take()
                for c in range(MC):
                    t = transpose(bank.ap[:, c * P:(c + 1) * P], v.ap[:, c * P:(c + 1) * P], after=[m, bank.free])
                v.release(t)
                state["mem_v"] = activation(mem_v[:, :, n * P:(n + 1) * P], bank.ap[:, 0:M].rearrange("p (c d) -> p c d", c=MC),
                                            ACT.Copy, after=[t])
                bank.release(state["mem_v"])
            state["a_read"] = [done]

        def projections():
            for h in range(H):
                if h:
                    yield from conv_qkv(h)
                    yield from conv_qkv(H + h)
                aside.extend([lambda: None] * (3 if h == 0 else 1))
                aside.extend(unit_norms(h))
                yield from conv_qkv(2 * H + h)
            for n in range(H):
                yield from spatial(n)
            norm = memory_norm()
            for n in range(H):
                if n != 1:
                    next(norm, None)
                yield from keep_gate(n)
            while aside:
                aside.pop(0)()
                yield

        heads_projected = []
        query, key, logits, filler = conv_qkv(0), conv_qkv(H), gates(), projections()
        for tile in (query, query, logits, key, key):
            next(tile)
        root, to_row = rstd_steps(EPS)
        root()
        next(filler)
        to_row()
        for part in (logits, logits, query, key):
            next(part, None)
        while convolved:
            convolved.pop(0)()
        for part in (filler, logits, filler, logits):
            next(part)
        in_flight, waiting = [], list(range(H))
        while waiting or in_flight:
            next(filler, None)
            if waiting and waiting[0] in heads_projected and len(in_flight) < 2:
                in_flight.append(delta_head(waiting.pop(0)))
            in_flight = [head for head in in_flight if next(head, "end") != "end"]

        def beside_recurrence():
            yield from filler
            yield from memory_keys_and_values()

        memory = beside_recurrence()
        for _ in recurrence():
            next(memory)
        delta_read = [state["o"]]
        state["b_read"] = [delta_read]
        outputs = head_outputs()
        for _ in outputs:
            next(memory, None)
        replaced = [[gate_ready[h] for h in range(H)], [b_ready[h] for h in range(H)]]
        marks = [load(xs[:, t, :], x_in[t], x_landed, after=replaced, lane=act) for t in range(KT)]
        x_ready = [marks[-1]] * KT
        for _ in memory:
            pass
        mem_k_ready, mem_v_ready = state["mem_k"], state["mem_v"]

        def residual(t, bank, done):
            m = tensor_tensor(xs[:, t, :], xs[:, t, :], bank.ap, ALU.add, after=[done, x_ready[t], x_read.get(t)])
            bank.release(m)
            x_ready[t] = m

        def next_norm(t, gain):
            a_ready[t] = stage_input(xs[:, t, :], column(gain, t), x_ready[t], a_hi[:, t, :], a_lo[:, t, :])
            m = stage_square(t, xs[:, t, :], x_ready[t], square_sum[:, :])
            x_read[t] = [a_ready[t], m]

        for n in range(KT):
            bank, done = project("w_out", n, *b_parts())
            state["b_read"] = [done]
            residual(n, bank, done)
            next_norm(n, "norm_xa")

        begin_between([("xa_wq", n) for n in range(2)], rstd_steps(EPS))
        xa_q = sbuf("xa_q", [P, KT, S], stack=cross)
        probs = Ring([sbuf(f"probs{i}", [P, NC, M], stack=cross)[:, :, :] for i in range(2)])
        probs_t = Ring([sbuf("probs_t", [P, MC, S], stack=cross)[:, :, :]])
        soft = [sbuf(f"soft{i}", [P, 4, NC], stack=cross) for i in range(2)]
        xa_q_ready, soft_free = {}, {}

        def attend(h):
            p = probs.take()
            biggest, bias, total, inverse = (soft[h % 2][:, i, :] for i in range(4))
            scale = XD ** -0.5
            q_ready = xa_q_ready[(h + 1) * XT - 1]
            two = [side_banks.take(), side_banks.take()]
            for c in range(NC):
                to = two[c // 2].ap[:, c % 2 * M:(c % 2 + 1) * M]
                for k in range(XT):
                    t = matmul(to, xa_q[:, h * XT + k, c * P:(c + 1) * P], mem_k[:, h * XT + k, :], k == 0, k == XT - 1,
                               after=[q_ready, mem_k_ready, two[c // 2].free], signal=(k == XT - 1))
                if c % 2:
                    m = reduce_max(biggest[:, c - 1:c + 1], two[c // 2].ap.rearrange("p (c m) -> p c m", m=M),
                                   after=[t, soft_free.get(h - 2)])
            m = tensor_scalar(bias, biggest, -scale, None, ALU.mult, after=[m])
            for c in range(NC):
                e = activation(p.ap[:, c, :], two[c // 2].ap[:, c % 2 * M:(c % 2 + 1) * M], ACT.Exp, after=[m, p.free],
                               bias=bias[:, c:c + 1], scale=scale, accum_out=total[:, c:c + 1])
                if c % 2:
                    two[c // 2].release(e)
            r = reciprocal(inverse, total, after=[e])
            m = tensor_tensor(p.ap, p.ap, along(inverse, M), ALU.mult, after=[r])
            soft_free[h] = m
            yield
            pt = probs_t.take()
            for c in range(MC):
                bank = side_banks.take()
                for s in range(NC):
                    t = transpose(bank.ap[:, s * P:(s + 1) * P], p.ap[:, s, c * P:(c + 1) * P], after=[m, bank.free])
                e = activation(pt.ap[:, c, :], bank.ap, ACT.Copy, after=[t, pt.free])
                bank.release(e)
            p.release(t)
            yield
            for d in range(XT):
                n = h * XT + d
                bank = side_banks.take()
                for c in range(MC):
                    t = matmul(bank.ap, mem_v[:, c, n * P:(n + 1) * P], pt.ap[:, c, :], c == 0, c == MC - 1,
                               after=[e, mem_v_ready, bank.free], signal=(c == MC - 1))
                bank.release(*split_to_b(n, bank.ap, t))
            pt.release(t)
            yield

        def cross_queries():
            hi, lo, ready = a_parts()
            for n in range(KT):
                bank, done = project("xa_wq", n, hi, lo, ready)
                state["a_read"] = [done]
                xa_q_ready[n] = leave(bank, done, xa_q[:, n, :])
                yield

        queries = cross_queries()
        pieces = iter(())
        for h in range(H):
            for _ in range(XT):
                next(queries)
                next(pieces, None)
            for _ in pieces:
                pass
            pieces = attend(h)
            next(pieces)
        known = b_parts()
        early = []
        for n in range(SPLIT_LEAD):
            early.append(Projection("xa_wo", n, known[0], known[1], b_ready.__getitem__))
            early[n].upto(KT - XT)
            next(pieces, None)
        for n in range(SPLIT_LEAD):
            begun["xa_wo", n] = early[n].upto(KT)
        hi, lo, ready = b_parts()
        for n in range(KT):
            bank, done = project("xa_wo", n, hi, lo, ready)
            state["b_read"] = [done]
            residual(n, bank, done)
            next_norm(n, "norm_ffn")
        begin_between([("ffn_w1", n) for n in range(2)], rstd_steps(EPS))
        cross.close()

        second = ExitStack()
        rope_cos = sbuf("rope_cos", [P, S], stack=second)
        rope_sin = sbuf("rope_sin", [P, S], stack=second)
        q2 = sbuf("q2", [P, QT, S], stack=second)
        k2 = sbuf("k2", [P, S], stack=second)
        v2 = sbuf("v2", [P, NC, P], stack=second)
        final = ExitStack()
        rstd1 = sbuf("rstd1", [P, S], stack=final)
        square_sum2 = sbuf("square_sum2", [P, S], stack=final)
        g12 = tensor_tensor(gain12[:, :], columns[:, COLUMNS["norm_final"][0]:COLUMNS["norm_final"][0] + KT],
                            columns[:, COLUMNS["norm_mix2"][0]:COLUMNS["norm_mix2"][0] + KT], ALU.mult)

        def rotary_tables():
            magic = 1.5 * 2.0 ** 23
            two_pi = [6.28125, float(np.float32(int((2 * np.pi - 6.28125) * 2 ** 21) / 2 ** 21))]
            two_pi.append(2 * np.pi - two_pi[0] - two_pi[1])
            angle, turns = temps.take(), temps.take()
            as_int = angle.ap.bitcast(I32)
            m = act.run(lambda e: e.dma_start(as_int, positions_in.partition_broadcast(P)), after=[angle.free],
                        counter=pos_landed, by=16)
            m = copy(turns.ap, as_int, after=[m, turns.free])
            m = tensor_scalar(angle.ap, turns.ap, column("inv_freq"), None, ALU.mult, after=[m])
            limit = float(np.nextafter(np.float32(np.pi), np.float32(0)))
            for to, quarter in ((rope_sin, 0.0), (rope_cos, 0.25)):
                r = tensor_scalar(turns.ap, angle.ap, float(1 / (2 * np.pi)), quarter, ALU.mult, ALU.add, after=[m])
                r = tensor_scalar(turns.ap, turns.ap, magic, None, ALU.add, after=[r])
                r = tensor_scalar(turns.ap, turns.ap, magic, None, ALU.subtract, after=[r])
                r = fused(to[:, :], turns.ap, -two_pi[0], angle.ap, ALU.mult, ALU.add, after=[r, cross_read])
                for part in two_pi[1:]:
                    r = fused(to[:, :], turns.ap, -part, to[:, :], ALU.mult, ALU.add, after=[r])
                r = tensor_scalar(to[:, :], to[:, :], float(quarter * 2 * np.pi), limit, ALU.add, ALU.min, after=[r])
                m = tensor_scalar(to[:, :], to[:, :], -limit, None, ALU.max, after=[r])
                a = activation(to[:, :], to[:, :], ACT.Sin, after=[m])
            angle.release(m)
            turns.release(m)
            state["tables"] = a

        def squared_relu(n, slot):
            hi, lo, ready = a_parts()
            bank, done = project("ffn_w1", n, hi, lo, ready)
            state["a_read"] = [done]
            t = temps.take()
            m = fused(t.ap, bank.ap, 0.0, rstd[:, :], ALU.max, ALU.mult, after=[done, state["rstd"], t.free])
            state["rstd_read"] = [m]
            bank.release(m)
            m = activation(t.ap, t.ap, ACT.Square, after=[m])
            t.release(*split_to_b(slot, t.ap, m))

        cross_read = [state["sum"]]
        for k0, k1 in FFN_PARTS:
            if k1 == FT:
                rotary_tables()
            for n in range(k0, k1):
                squared_relu(n, n - k0)
            hi, lo, ready = b_parts(lambda k, k0=k0: k - k0)
            for n in range(KT):
                bank, done = project("ffn_w2", n, hi, lo, ready, k0, k1)
                state["b_read"] = [done]
                residual(n, bank, done)
                if k1 == FT:
                    a_ready[n] = stage_input(xs[:, n, :], gain12[:, n:n + 1], [x_ready[n], g12], a_hi[:, n, :], a_lo[:, n, :])
                    m = stage_square(n, xs[:, n, :], x_ready[n], square_sum[:, :])
                    m2 = stage_square(n, xs[:, n, :], x_ready[n], square_sum2[:, :], scale=column("norm_final", n), key="sum2")
                    x_read[n] = [a_ready[n], m, m2]

        def both_roots():
            one, r1, t = token_root(square_sum[:, :], state["sum"], 1.0 / D, EPS)
            state["sum_read"] = [t]
            bank, t = token_sums(square_sum2[:, :], state["sum2"])
            two, both = narrow.take(), narrow.take()
            one_, two_, both_ = (slot.ap[:, 0:NC] for slot in (one, two, both))
            m = tensor_tensor(both_, one_, one_, ALU.mult, after=[r1, both.free])
            m = fused(two_, bank.ap[:, 0:NC], 1.0 / D, both_, ALU.mult, ALU.mult, after=[t, m, two.free])
            bank.release(m)
            m = tensor_scalar(two_, two_, EPS_2, None, ALU.add, after=[m])
            m = power(two_, m)
            r = tensor_tensor(both_, one_, two_, ALU.mult, after=[m], lane=pool)
            two.release(r)
            state["roots"] = one, both, r

        def both_to_rows():
            one, both, r = state["roots"]
            state["rstd"] = spread_to(rstd[:, :], both, r, state["rstd_read"])
            state["rstd1"] = spread_to(rstd1[:, :], one, r, [])

        begin_between([("q2", n) for n in range(2)], (both_roots, both_to_rows))
        r1 = state["rstd1"]

        def normed_residual(n):
            x_ready[n] = fused(xs[:, n, :], xs[:, n, :], column("norm_final", n), rstd1[:, :], ALU.mult, ALU.mult,
                               after=[x_read[n], r1])
            x_read[n] = []

        hi, lo, ready = a_parts()
        q2_ready = {}

        def rotated(name, n, to, bias):
            bank, done = project(name, n, hi, lo, ready)
            m = leave(bank, done, to)
            m = activation(to, to, ACT.Identity, after=[m], bias=bias)
            yield
            bank = side_banks.take()
            t = matmul(bank.ap, rotate, to, after=[m, bank.free])
            other = temps.take()
            o = tensor_tensor(other.ap, bank.ap, rope_sin[:, :], ALU.mult, after=[t, state["tables"], other.free])
            bank.release(o)
            m = tensor_tensor(to, to, rope_cos[:, :], ALU.mult, after=[t, state["tables"]], lane=pool)
            m = tensor_tensor(to, to, other.ap, ALU.add, after=[m, o], lane=pool)
            other.release(m)
            q2_ready[name, n] = m

        turning = iter(())
        for name, n, to, bias in [("q2", n, q2[:, n, :], column("b_q", n)) for n in range(QT)] + [
                ("k2", 0, k2[:, :], column("b_k"))]:
            following = rotated(name, n, to, bias)
            next(following)
            next(turning, None)
            turning = following
            if name == "q2":
                normed_residual(n)
        bank, done = project("v2", 0, hi, lo, ready)
        next(turning, None)
        k2_ready = q2_ready["k2", 0]
        v = temps.take()
        m = leave(bank, done, v.ap, v.free)
        m = activation(v.ap, v.ap, ACT.Identity, after=[m], bias=column("b_v"))
        bank = side_banks.take()
        for c in range(NC):
            t = transpose(bank.ap[:, c * P:(c + 1) * P], v.ap[:, c * P:(c + 1) * P], after=[m, bank.free])
        v.release(t)
        v2_ready = activation(v2[:, :, :], chunked(bank.ap), ACT.Copy, after=[t])
        bank.release(v2_ready)
        for n in range(QT, KT):
            normed_residual(n)
        residual_ready = [x_ready[KT - 1]]
        final.close()
        merged = sbuf("merged", [P, KT, S], stack=second)
        scores2 = Ring([sbuf(f"scores2_{i}", [P, 2 * 2 * P], stack=second)[:, :] for i in range(2)])
        probs2_t = sbuf("probs2_t", [P, 2, QT, P], stack=second)
        soft2 = [sbuf(f"soft2_{i}", [P, 5, 2], stack=second) for i in range(2)]
        band = matrices[:, BAND:BAND + 2, :].rearrange("p a k -> p (a k)")

        def window_scores(count, n, g, pair):
            halves = 1 if n == 0 else 2
            width = P * halves
            part = slice(g * HD, (g + 1) * HD)
            w = scores2.take()
            s = w.ap[:, 0:2 * width].rearrange("p (h k) -> p h k", h=2)
            biggest, bias, total, sink, inverse = (soft2[count % 2][:, i, :] for i in range(5))
            own_sinks = sinks[:, g * QT + 2 * pair:g * QT + 2 * pair + 2]
            bank = side_banks.take()
            b = bank.ap[:, 0:2 * width].rearrange("p (h k) -> p h k", h=2)
            for i in range(2):
                t = matmul(b[:, i, :], q2[part, 2 * pair + i, n * P:(n + 1) * P], k2[part, (n + 1) * P - width:(n + 1) * P],
                           after=[q2_ready["q2", 2 * pair + i], k2_ready, bank.free])
            mask = over_tokens(band[:, 2 * P - width:2 * P], 2)
            m = fused(s, b, HD ** -0.5, mask, ALU.mult, ALU.add, after=[t, w.free, residual_ready])
            bank.release(m)
            m = reduce_max(biggest, s, after=[m, soft2_free.get(count - 2)])
            m = tensor_tensor(biggest, biggest, own_sinks, ALU.max, after=[m])
            bias_ok = tensor_scalar(bias, biggest, -1.0, None, ALU.mult, after=[m])
            m = tensor_tensor(sink, own_sinks, bias, ALU.add, after=[bias_ok])
            for i in range(2):
                e = activation(s[:, i, :], s[:, i, :], ACT.Exp, after=[bias_ok], bias=bias[:, i:i + 1],
                               accum_out=total[:, i:i + 1])
            e = activation(sink, sink, ACT.Exp, after=[m])
            m = tensor_tensor(total, total, sink, ALU.add, after=[e])
            m = reciprocal(inverse, total, after=[m])
            soft2_free[count] = tensor_tensor(s, s, along(inverse, width), ALU.mult, after=[m], lane=pool)
            return w, s, halves, pair, soft2_free[count]

        def window_turn(w, s, halves, pair, m):
            bank = side_banks.take()
            b = bank.ap[:, 0:2 * P * halves].rearrange("p (a h q) -> p a h q", a=halves, h=2)
            for a in range(halves):
                for i in range(2):
                    t = transpose(b[:, a, i, :], s[:, i, a * P:(a + 1) * P], after=[m, bank.free])
            w.release(t)
            for a in range(halves):
                e = activation(probs2_t[:, a, 2 * pair:2 * pair + 2, :], b[:, a, :, :], ACT.Copy,
                               after=[t, state["probs2_read"], residual_ready])
            bank.release(e)
            return e

        soft2_free = {}

        def window_attention():
            pairs = [(n, g, pair) for n in range(NC) for g in range(KVH) for pair in range(QT // 2)]
            state["probs2_read"] = []
            scored = window_scores(0, *pairs[0])
            yield
            for count, (n, g, pair) in enumerate(pairs):
                now = scored
                if count + 1 < len(pairs):
                    scored = window_scores(count + 1, *pairs[count + 1])
                e = window_turn(*now)
                yield
                if pair == QT // 2 - 1:
                    part, halves = slice(g * HD, (g + 1) * HD), now[2]
                    bank = side_banks.take()
                    for a in range(halves):
                        t = matmul(bank.ap[part, :], v2[:, n - halves + 1 + a, part],
                                   probs2_t[:, a, :, :].rearrange("p h q -> p (h q)"), a == 0, a == halves - 1,
                                   after=[e, v2_ready, bank.free], signal=(a == halves - 1))
                    state["probs2_read"] = [t]
                    o = copy(q2[part, :, n * P:(n + 1) * P], bank.ap[part, :].rearrange("p (h q) -> p h q", h=QT), after=[t])
                    bank.release(o)
                    yield
            state["attended"] = o

        def gated_conv(n):
            bank, done = project("cc2", n, hi, lo, ready)
            cc = temps.take()
            m = leave(bank, done, cc.ap, cc.free)
            yield
            bank, done = project("cx2", n, hi, lo, ready)
            cx = temps.take()
            m = leave(bank, done, cx.ap, cx.free)
            m = activation(cx.ap, cx.ap, ACT.Identity, after=[m], bias=column("b_cx", n))
            m = fused(cc.ap, cc.ap, column("b_cc", n), cx.ap, ALU.add, ALU.mult, after=[m])
            cx.free = [m]
            y = causal_conv(cc, m, cx, TAPS2, lambda i: column("conv_mix", i * KT + n))
            yield
            bank, done = project("cb2", n, hi, lo, ready)
            cb = temps.take()
            m = leave(bank, done, cb.ap, cb.free)
            m = fused(cx.ap, cb.ap, column("b_cb", n), cx.ap, ALU.add, ALU.mult, after=[m, y])
            cb.release(m)
            cx.release(*split_to_b(n, cx.ap, m))
            yield

        def conv_branch():
            for n in range(KT):
                yield from gated_conv(n)
            b_hi_, b_lo_, b_ok = b_parts()
            for n in range(KT):
                bank, done = project("gc2", n, hi, lo, ready)
                gate_t = temps.take()
                m = leave(bank, done, gate_t.ap, gate_t.free)
                m = activation(gate_t.ap, gate_t.ap, ACT.Sigmoid, after=[m], bias=column("b_gc", n))
                yield
                bank, done = project("conv_out2", n, b_hi_, b_lo_, b_ok)
                state["b_read"] = [done]
                merged_ready[n] = tensor_tensor(merged[:, n, :], bank.ap, gate_t.ap, ALU.mult, after=[done, m, residual_ready])
                bank.release(merged_ready[n])
                gate_t.release(merged_ready[n])
                yield

        merged_ready = {}
        interleave(conv_branch(), window_attention(), 5 * KT, NC * KVH * 3 + 1)
        for t in range(QT):
            split_to_b(t, q2[:, t, :], state["attended"])
        b_hi_, b_lo_, b_ok = b_parts()
        attn_marks = [b_ready[t] for t in range(QT)]
        merged_tile = lambda n: (n + QT) % KT

        def merge_parts(n):
            b_ready[merged_tile(n)] = split_parts(merged[:, n, :], b_hi[:, merged_tile(n), :], b_lo[:, merged_tile(n), :],
                                                  [merged_ready[n], state["b_read"]])

        conv_read = state["b_read"]
        for n in range(KT):
            bank, done = project("ga2", n, hi, lo, ready)
            state["a_read"] = [done]
            gate_t = temps.take()
            m = leave(bank, done, gate_t.ap, gate_t.free)
            m = activation(gate_t.ap, gate_t.ap, ACT.Sigmoid, after=[m], bias=column("b_ga", n))
            bank, done = project("attn_out2", n, b_hi_, b_lo_, b_ok, 0, QT)
            m = fused(gate_t.ap, bank.ap, column("b_attn_out", n), gate_t.ap, ALU.add, ALU.mult, after=[done, m])
            bank.release(m)
            merged_ready[n] = tensor_tensor(merged[:, n, :], merged[:, n, :], gate_t.ap, ALU.add, after=[m, merged_ready[n]])
            gate_t.release(merged_ready[n])
            if n < KT - QT:
                merge_parts(n)
        state["b_read"] = [done]
        for n in range(KT - QT, KT):
            merge_parts(n)
        hi, lo, ready = b_parts(merged_tile)
        for n in range(KT):
            bank, done = project("mix2", n, hi, lo, ready)
            state["b_read"] = [done]
            residual(n, bank, done)
            next_norm(n, "norm_ffn2")
        begin_between([("up2", 0), ("gate2", 0)], rstd_steps(EPS_2))
        second.close()

        hi, lo, ready = a_parts()
        for k0, k1 in FFN2_PARTS:
            for n in range(k0, k1):
                bank, done = project("up2", n, hi, lo, ready)
                up = temps.take()
                m = leave(bank, done, up.ap, up.free)
                y = temps.take()
                m = causal_conv(up, m, y, TAPS2, lambda i: column("ffn_conv", i * F2T + n))
                s = activation(y.ap, y.ap, ACT.Silu, after=[m], bias=column("ffn_conv_b", n))
                bank, done = project("gate2", n, hi, lo, ready)
                g = temps.take()
                m = leave(bank, done, g.ap, g.free)
                m = tensor_tensor(y.ap, y.ap, g.ap, ALU.mult, after=[m, s])
                g.release(m)
                y.release(*split_to_b(n - k0, y.ap, m))
            b_hi_, b_lo_, b_ok = b_parts(lambda k, k0=k0: k - k0)
            for n in range(KT):
                bank, done = project("down2", n, b_hi_, b_lo_, b_ok, k0, k1)
                state["b_read"] = [done]
                residual(n, bank, done)
                if k1 == F2T:
                    x_read[n] = [stage_square(n, xs[:, n, :], x_ready[n], square_sum[:, :], lane=dve)]
        slot, r, t = token_root(square_sum[:, :], state["sum"], 1.0 / D, EPS_2)
        bank, t = spread(slot.ap, r)
        for n in range(KT):
            x_ready[n] = fused(xs[:, n, :], xs[:, n, :], column("norm_final2", n), bank.ap, ALU.mult, ALU.mult,
                               after=[t, x_read[n]])
        finish()


def tiled(w):
    k, n = w.shape
    return w.reshape(k // P, P, n // P, P).transpose(2, 0, 1, 3)


def paired_heads(w, axis):
    shape = list(w.shape)
    parts = shape[:axis] + [KVH, QT, HD] + shape[axis + 1:]
    return np.swapaxes(w.reshape(parts), axis, axis + 1).reshape(shape)


def kernel(**inputs):
    import concourse.bacc as bacc
    from concourse.bass_utils import run_bass_kernel_spmd

    a = {name: np.asarray(value) for name, value in inputs.items()}
    w_in, w_in_2 = a["w_in"][0], a["w_in_2"][0]
    width = H * P
    logits = np.concatenate([w_in[:, 6 * width:], np.zeros((D, P - 2 * H), np.float32)], axis=1)
    at = np.cumsum([0, D, D, D, QH * HD, KVH * HD, KVH * HD, D, D])
    cb, cc, cx, q, k, v, gc, ga = (w_in_2[:, i:j] for i, j in zip(at[:-1], at[1:]))
    b_cb, b_cc, b_cx, b_q, b_k, b_v, b_gc, b_ga = (a["b_in_2"][0, i:j] for i, j in zip(at[:-1], at[1:]))
    units = {
        "gu": tiled(w_in[:, 0:width]), "gv": tiled(w_in[:, width:2 * width]),
        "qkv": tiled(w_in[:, 2 * width:5 * width]), "logits": tiled(logits), "gate": tiled(w_in[:, 5 * width:6 * width]),
        "w_out": tiled(a["w_out"][0]), "xa_wq": tiled(a["xa_wq"][0]), "xa_wk": tiled(a["xa_wk"][0]),
        "xa_wv": tiled(a["xa_wv"][0]), "xa_wo": tiled(a["xa_wo"][0]), "ffn_w1": tiled(a["ffn_w1"][0]),
        "ffn_w2": tiled(a["ffn_w2"][0]), "cb2": tiled(cb), "cc2": tiled(cc), "cx2": tiled(cx),
        "q2": tiled(paired_heads(q, 1)), "k2": tiled(k), "v2": tiled(v), "gc2": tiled(gc), "ga2": tiled(ga),
        "conv_out2": tiled(a["w_conv_out_2"][0]), "attn_out2": tiled(paired_heads(a["w_attn_out_2"][0], 0)),
        "mix2": tiled(a["w_mix_out_2"][0]), "up2": tiled(a["w_ffn_up_2"][0][:, :F2T * P]),
        "gate2": tiled(a["w_ffn_up_2"][0][:, F2T * P:]), "down2": tiled(a["w_ffn_down_2"][0]),
    }
    stream = [units[name][n, k0:k1] for name, n, k0, k1 in WEIGHT_ORDER]
    spare = N_BLOCKS * UNITS_PER_BLOCK - N_UNITS
    stream.append(np.zeros((spare, P, P), np.float32))
    weights = np.concatenate(stream).reshape(N_BLOCKS, UNITS_PER_BLOCK, P, P).transpose(0, 2, 1, 3)

    def cols(vector):
        return vector.reshape(-1, P).T

    taps = lambda w: np.concatenate([cols(w[i]) for i in range(w.shape[0])], axis=1)
    inv_freq = (10000.0 ** (-np.arange(0, HD, 2, dtype=np.float32) / HD)).astype(np.float32)
    constant = {"inv_freq": np.tile(inv_freq, P // len(inv_freq))[:, None],
                "minus_half": np.full((P, 1), -0.5, np.float32)}
    vectors = {
        "norm_mix": cols(a["norm_mix"]), "norm_xa": cols(a["norm_xa"]), "norm_mem": cols(a["norm_mem"]),
        "norm_ffn": cols(a["norm_ffn"]), "norm_final": cols(a["norm_final"]), "norm_mix2": cols(a["norm_mix_w_2"]),
        "norm_ffn2": cols(a["norm_ffn_w_2"]), "norm_final2": cols(a["norm_final_w_2"]),
        "dn_conv": taps(a["dn_conv"][0]), "dn_onorm": cols(a["dn_onorm"]),
        "ln_g": cols(a["gm_ln_g"]), "ln_b": cols(a["gm_ln_b"]),
        "b_cb": cols(b_cb), "b_cc": cols(b_cc), "b_cx": cols(b_cx), "b_q": cols(paired_heads(b_q, 0)),
        "b_k": cols(b_k), "b_v": cols(b_v), "b_gc": cols(b_gc), "b_ga": cols(b_ga),
        "conv_mix": taps(a["conv_mix_w_2"][0]), "b_attn_out": cols(a["b_attn_out_2"]),
        "ffn_conv": taps(a["ffn_conv_w_2"][0]), "ffn_conv_b": cols(a["ffn_conv_b_2"]), **constant,
    }
    rows = {"gm_bs": a["gm_bs"], "a_log": a["dn_a_log"],
            "dt_bias": a["dn_dt_bias"]}
    arrays = {
        "x_in": a["x"][0].T.reshape(KT, P, S),
        "mem_in": a["mem"][0].T.reshape(KT, P, M).transpose(1, 0, 2),
        "weights_in": weights.reshape(N_BLOCKS, P, UNITS_PER_BLOCK * P),
        "ws_in": a["gm_ws"][0].transpose(2, 0, 1),
        "columns_in": np.concatenate([vectors[name] for name in COLUMNS], axis=1),
        "rows_in": np.concatenate([rows[name].reshape(-1) for name in ROWS]),
        "sinks_in": a["sinks_2"][0],
        "matrices_in": constant_matrices(),
        "positions_in": a["positions_2"][0],
    }
    arrays = {name: np.ascontiguousarray(value) for name, value in arrays.items()}
    nc = bacc.Bacc("TRN2", target_bir_lowering=False, num_devices=1)
    args = [nc.dram_tensor(name, v.shape, mybir.dt.from_np(v.dtype), kind="ExternalInput").ap()
            for name, v in arrays.items()]
    out = nc.dram_tensor("out", (KT, P, S), F32, kind="ExternalOutput").ap()
    build_program(nc, *args, out)
    result = run_bass_kernel_spmd(nc, [arrays], core_ids=[0]).results[0]["out"]
    return np.ascontiguousarray(result.reshape(D, S).T)[None]
```
